# Optimizing a Trainium2 kernel written in Bass

```python
import math
import jax, jax.numpy as jnp
from jax import lax
import numpy as np

D_MODEL = 1024
BATCH = 1
SEQ = 1024
DEPTH = 1

N_MIXERS = 4
EPS = 1e-6
LN_EPS = 1e-5
CHUNK = 128
D_FF = 4 * D_MODEL

GM_WIDTH = 2 * D_MODEL
GM_GROUPS = 8
GM_GDIM = GM_WIDTH // GM_GROUPS

S5_WIDTH = D_MODEL
S5_GROUP = 16
S5_GROUPS = S5_WIDTH // S5_GROUP
S5_STATE = 64
S5_DT_MIN = 1e-3
S5_DT_MAX = 1e-1

RET_HEADS = max(4, D_MODEL // 256)
RET_DK = D_MODEL // RET_HEADS
RET_DV = 2 * RET_DK
RET_QD = RET_HEADS * RET_DK
RET_VD = RET_HEADS * RET_DV
ROPE_BASE = 10000.0

SC_WIDTH = D_MODEL
CONV_WIDTH = 3

kernel_name = "interleaved_hybrid_gmlp_s5_retnet_shortconv"

def _n_uses(m):
    return len(range(m, DEPTH, N_MIXERS))

def rms_norm(x, g):
    xf = x.astype(jnp.float32)
    y = xf * lax.rsqrt(jnp.mean(xf * xf, axis=-1, keepdims=True) + EPS)
    return (y * g.astype(jnp.float32)).astype(x.dtype)

def gmlp_mixer(h, w_in, ln_g, w_s, b_s, w_out):
    b, l, _ = h.shape
    z = jax.nn.gelu(h @ w_in)
    u, v = jnp.split(z, 2, axis=-1)
    vf = v.astype(jnp.float32)
    mu = jnp.mean(vf, axis=-1, keepdims=True)
    var = jnp.mean(jnp.square(vf - mu), axis=-1, keepdims=True)
    v = ((vf - mu) * lax.rsqrt(var + LN_EPS) * ln_g.astype(jnp.float32)).astype(h.dtype)
    v = v.reshape(b, l // CHUNK, CHUNK, GM_GROUPS, GM_GDIM)
    causal = jnp.tril(jnp.ones((CHUNK, CHUNK), dtype=bool))
    ws = jnp.where(causal[None], w_s, jnp.zeros_like(w_s))
    sv = jnp.einsum('gts,bnsge->bntge', ws, v) + b_s.T[None, None, :, :, None]
    return (u * sv.reshape(b, l, GM_WIDTH)) @ w_out

def _complex_combine(e1, e2):
    a1r, a1i, b1r, b1i = e1
    a2r, a2i, b2r, b2i = e2
    return (a2r * a1r - a2i * a1i,
            a2r * a1i + a2i * a1r,
            a2r * b1r - a2i * b1i + b2r,
            a2r * b1i + a2i * b1r + b2i)

def s5_mixer(h, w_in, log_dt, a_re, a_im, b_re, b_im, c_re, c_im, d_skip, w_glu):
    f32 = jnp.float32
    b, l, _ = h.shape
    u = (h @ w_in).astype(f32)
    dt = jnp.exp(log_dt.astype(f32))[:, None]
    ar, ai = a_re.astype(f32), a_im.astype(f32)
    mag = jnp.exp(ar * dt)
    ang = ai * dt
    abar_r, abar_i = mag * jnp.cos(ang), mag * jnp.sin(ang)
    den = ar * ar + ai * ai
    nr, ni = abar_r - 1.0, abar_i
    cr = (nr * ar + ni * ai) / den
    ci = (ni * ar - nr * ai) / den
    br, bi = b_re.astype(f32), b_im.astype(f32)
    bbar_r = cr[..., None] * br - ci[..., None] * bi
    bbar_i = cr[..., None] * bi + ci[..., None] * br
    cre, cim = c_re.astype(f32), c_im.astype(f32)

    uc = u.reshape(b, l // CHUNK, CHUNK, S5_GROUPS, S5_GROUP).transpose(1, 0, 2, 3, 4)

    def step(carry, u_chunk):
        hr0, hi0 = carry
        bu_r = jnp.einsum('gpm,bcgm->bcgp', bbar_r, u_chunk)
        bu_i = jnp.einsum('gpm,bcgm->bcgp', bbar_i, u_chunk)
        a_r = jnp.broadcast_to(abar_r, bu_r.shape)
        a_i = jnp.broadcast_to(abar_i, bu_i.shape)
        pr, pi, sr, si = lax.associative_scan(_complex_combine, (a_r, a_i, bu_r, bu_i), axis=1)
        hr = pr * hr0[:, None] - pi * hi0[:, None] + sr
        hi = pr * hi0[:, None] + pi * hr0[:, None] + si
        y = jnp.einsum('gmp,bcgp->bcgm', cre, hr) - jnp.einsum('gmp,bcgp->bcgm', cim, hi)
        return (hr[:, -1], hi[:, -1]), y

    init = (jnp.zeros((b, S5_GROUPS, S5_STATE), f32), jnp.zeros((b, S5_GROUPS, S5_STATE), f32))
    _, y = lax.scan(step, init, uc)
    y = y.transpose(1, 0, 2, 3, 4).reshape(b, l, S5_WIDTH) + d_skip.astype(f32) * u
    z = jax.nn.gelu(y).astype(h.dtype)
    val, gate = jnp.split(z @ w_glu, 2, axis=-1)
    return val * jax.nn.sigmoid(gate)

def _rotate(t, cos, sin):
    t1, t2 = jnp.split(t, 2, axis=-1)
    return jnp.concatenate([t1 * cos - t2 * sin, t1 * sin + t2 * cos], axis=-1)

def retention_mixer(h, w_in, gn_g, w_out):
    f32 = jnp.float32
    b, l, _ = h.shape
    n = l // CHUNK
    proj = h @ w_in
    q, k, v, g = jnp.split(proj, [RET_QD, 2 * RET_QD, 2 * RET_QD + RET_VD], axis=-1)
    q = q.astype(f32).reshape(b, l, RET_HEADS, RET_DK)
    k = k.astype(f32).reshape(b, l, RET_HEADS, RET_DK)
    v = v.astype(f32).reshape(b, l, RET_HEADS, RET_DV)
    pos = jnp.arange(l, dtype=f32)
    inv_freq = ROPE_BASE ** (-jnp.arange(0, RET_DK, 2, dtype=f32) / RET_DK)
    theta = pos[:, None] * inv_freq[None, :]
    cos, sin = jnp.cos(theta)[:, None, :], jnp.sin(theta)[:, None, :]
    q = _rotate(q, cos, sin)
    k = _rotate(k, cos, sin) * (RET_DK ** -0.5)

    log_g = jnp.log(1.0 - 2.0 ** (-5.0 - jnp.arange(RET_HEADS, dtype=f32)))
    idx = jnp.arange(CHUNK, dtype=f32)
    diff = idx[:, None] - idx[None, :]
    dmask = jnp.where(diff[None] >= 0, jnp.exp(jnp.maximum(diff, 0.0)[None] * log_g[:, None, None]), 0.0)
    xi = jnp.exp((idx[None, :] + 1.0) * log_g[:, None])[..., None]
    zeta = jnp.exp((CHUNK - 1.0 - idx[None, :]) * log_g[:, None])[..., None]
    chunk_decay = jnp.exp(CHUNK * log_g)[:, None, None]

    def to_chunks(t):
        return t.reshape(b, n, CHUNK, RET_HEADS, t.shape[-1]).transpose(1, 0, 3, 2, 4)

    def step(R, qkv):
        qc, kc, vc = qkv
        s = jnp.einsum('bhtd,bhsd->bhts', qc, kc) * dmask
        inner = jnp.einsum('bhts,bhsv->bhtv', s, vc)
        cross = jnp.einsum('bhtd,bhdv->bhtv', qc, R) * xi
        R_new = chunk_decay * R + jnp.einsum('bhsd,bhsv->bhdv', kc * zeta, vc)
        return R_new, inner + cross

    R0 = jnp.zeros((b, RET_HEADS, RET_DK, RET_DV), f32)
    _, o = lax.scan(step, R0, (to_chunks(q), to_chunks(k), to_chunks(v)))
    o = o.transpose(1, 0, 3, 2, 4).reshape(b, l, RET_HEADS, RET_DV)
    mu = jnp.mean(o, axis=-1, keepdims=True)
    var = jnp.mean(jnp.square(o - mu), axis=-1, keepdims=True)
    o = ((o - mu) * lax.rsqrt(var + LN_EPS)).reshape(b, l, RET_VD) * gn_g.astype(f32)
    return (jax.nn.silu(g) * o.astype(h.dtype)) @ w_out

def shortconv_mixer(h, w_in, conv_w, w_out):
    gate_b, gate_c, xin = jnp.split(h @ w_in, 3, axis=-1)
    z = gate_c * xin
    y = lax.conv_general_dilated(z, conv_w, window_strides=(1,), padding=[(CONV_WIDTH - 1, 0)],
                                 dimension_numbers=('NWC', 'WIO', 'NWC'),
                                 feature_group_count=SC_WIDTH)
    return (gate_b * y) @ w_out

def channel_mlp(h, w1, w2):
    return jnp.square(jax.nn.relu(h @ w1)) @ w2

def setup_inputs(seed: int = 0) -> dict:
    key = jax.random.key(seed)
    ks = iter(jax.random.split(key, 40))
    f32 = jnp.float32
    nA, nB, nC, nD = _n_uses(0), _n_uses(1), _n_uses(2), _n_uses(3)

    def nrm(shape, std):
        return jax.random.normal(next(ks), shape, f32) * std

    def gain(shape):
        return 1.0 + 0.02 * jax.random.normal(next(ks), shape, f32)

    x = jax.random.normal(next(ks), (BATCH, SEQ, D_MODEL), f32)
    norm1_g = gain((DEPTH, D_MODEL))
    norm2_g = gain((DEPTH, D_MODEL))
    mlp_w1 = nrm((DEPTH, D_MODEL, D_FF), D_MODEL ** -0.5)
    mlp_w2 = nrm((DEPTH, D_FF, D_MODEL), D_FF ** -0.5)
    final_g = gain((D_MODEL,))

    a_w_in = nrm((nA, D_MODEL, 2 * GM_WIDTH), D_MODEL ** -0.5)
    a_ln_g = gain((nA, GM_WIDTH))
    a_ws = nrm((nA, GM_GROUPS, CHUNK, CHUNK), CHUNK ** -0.5)
    a_bs = gain((nA, GM_GROUPS, CHUNK))
    a_w_out = nrm((nA, GM_WIDTH, D_MODEL), GM_WIDTH ** -0.5)

    b_w_in = nrm((nB, D_MODEL, S5_WIDTH), D_MODEL ** -0.5)
    b_log_dt = jax.random.uniform(next(ks), (nB, S5_GROUPS), f32,
                                  math.log(S5_DT_MIN), math.log(S5_DT_MAX))
    b_a_re = -0.5 + 0.01 * jax.random.normal(next(ks), (nB, S5_GROUPS, S5_STATE), f32)
    b_a_im = (math.pi * jnp.arange(S5_STATE, dtype=f32))[None, None, :] \
        + 0.01 * jax.random.normal(next(ks), (nB, S5_GROUPS, S5_STATE), f32)
    b_b_re = nrm((nB, S5_GROUPS, S5_STATE, S5_GROUP), (2 * S5_GROUP) ** -0.5)
    b_b_im = nrm((nB, S5_GROUPS, S5_STATE, S5_GROUP), (2 * S5_GROUP) ** -0.5)
    b_c_re = nrm((nB, S5_GROUPS, S5_GROUP, S5_STATE), (2 * S5_STATE) ** -0.5)
    b_c_im = nrm((nB, S5_GROUPS, S5_GROUP, S5_STATE), (2 * S5_STATE) ** -0.5)
    b_d = nrm((nB, S5_WIDTH), 1.0)
    b_w_glu = nrm((nB, S5_WIDTH, 2 * D_MODEL), S5_WIDTH ** -0.5)

    c_w_in = nrm((nC, D_MODEL, 2 * RET_QD + 2 * RET_VD), D_MODEL ** -0.5)
    c_gn_g = gain((nC, RET_VD))
    c_w_out = nrm((nC, RET_VD, D_MODEL), RET_VD ** -0.5)

    d_w_in = nrm((nD, D_MODEL, 3 * SC_WIDTH), D_MODEL ** -0.5)
    d_conv_w = nrm((nD, CONV_WIDTH, 1, SC_WIDTH), CONV_WIDTH ** -0.5)
    d_w_out = nrm((nD, SC_WIDTH, D_MODEL), SC_WIDTH ** -0.5)

    return {"x": x, "norm1_g": norm1_g, "norm2_g": norm2_g, "mlp_w1": mlp_w1, "mlp_w2": mlp_w2,
            "final_g": final_g,
            "a_w_in": a_w_in, "a_ln_g": a_ln_g, "a_ws": a_ws, "a_bs": a_bs, "a_w_out": a_w_out,
            "b_w_in": b_w_in, "b_log_dt": b_log_dt, "b_a_re": b_a_re, "b_a_im": b_a_im,
            "b_b_re": b_b_re, "b_b_im": b_b_im, "b_c_re": b_c_re, "b_c_im": b_c_im,
            "b_d": b_d, "b_w_glu": b_w_glu,
            "c_w_in": c_w_in, "c_gn_g": c_gn_g, "c_w_out": c_w_out,
            "d_w_in": d_w_in, "d_conv_w": d_conv_w, "d_w_out": d_w_out}

def reference(x, norm1_g, norm2_g, mlp_w1, mlp_w2, final_g,
              a_w_in, a_ln_g, a_ws, a_bs, a_w_out,
              b_w_in, b_log_dt, b_a_re, b_a_im, b_b_re, b_b_im, b_c_re, b_c_im, b_d, b_w_glu,
              c_w_in, c_gn_g, c_w_out,
              d_w_in, d_conv_w, d_w_out):
    for i in range(DEPTH):
        m, j = i % N_MIXERS, i // N_MIXERS
        hn = rms_norm(x, norm1_g[i])
        if m == 0:
            y = gmlp_mixer(hn, a_w_in[j], a_ln_g[j], a_ws[j], a_bs[j], a_w_out[j])
        elif m == 1:
            y = s5_mixer(hn, b_w_in[j], b_log_dt[j], b_a_re[j], b_a_im[j], b_b_re[j], b_b_im[j],
                         b_c_re[j], b_c_im[j], b_d[j], b_w_glu[j])
        elif m == 2:
            y = retention_mixer(hn, c_w_in[j], c_gn_g[j], c_w_out[j])
        else:
            y = shortconv_mixer(hn, d_w_in[j], d_conv_w[j], d_w_out[j])
        x = x + y.astype(x.dtype)
        x = x + channel_mlp(rms_norm(x, norm2_g[i]), mlp_w1[i], mlp_w2[i]).astype(x.dtype)
    return rms_norm(x, final_g)


_drawn_inputs = setup_inputs


def setup_inputs(seed=0):
    import zlib

    import numpy as np

    out = dict(_drawn_inputs(seed))
    spreads = {}
    factors = {'norm1_g': 3.225, 'norm2_g': 12.56, 'final_g': 7.244, 'a_ln_g': 29.432, 'a_bs': 19.6}
    for name, (base, spread) in spreads.items():
        noise = np.random.default_rng([zlib.crc32(name.encode()), seed]).standard_normal(out[name].shape)
        drawn = base * np.exp(spread * noise) if base else spread * noise
        out[name] = __import__('jax').numpy.asarray(drawn.astype(out[name].dtype))
    for name, factor in factors.items():
        out[name] = (out[name] * factor).astype(out[name].dtype)
    return out
```

```python
from contextlib import ExitStack

import concourse.bass as bass
from concourse import mybir

F32 = mybir.dt.float32
F32R = mybir.dt.float32r
ALU = mybir.AluOpType
ACT = mybir.ActivationFunctionType

P = 128
T = 1024
D = 1024
W = 2 * D
F = 4 * D
GROUPS = 8
NB = 512
MT = T // P
KT = D // P
JT = W // P
HALF = T // NB
BANKS = 8
JB = NB // P
RING = 4
AHEAD = RING - 1
PAIRS = 4
SCRATCH = 4
EPS = 1e-6
LN_EPS = 1e-5

G_V, G_U, G_OUT, G_MLP = 0, W // NB, 2 * W // NB, 2 * W // NB + 2 * D // NB
MLP_BLOCKS = F // (8 * P)
N_GROUPS = G_MLP + 4 * MLP_BLOCKS
TILES = 8 * N_GROUPS

FILL_X = 1
FILL_V = FILL_X + 2 * KT
FILL_WS = FILL_V + 8 * 4
FILL_U = FILL_WS + 2
FILL_OUT = FILL_U + 16 * 4
FILL_MLP = FILL_OUT + 16 * 2
AR_V = 2 * KT
AR_U = AR_V + 8 * 4
AR_OUT = AR_U + 8 * 4
AR_MLP = AR_OUT + 8 * 2
DR_X = 1
DR_V = DR_X + 2 * KT
DR_U = DR_V + 2
DR_OUT = DR_U + 8 * 4
DR_MLP = DR_OUT + 16 * 2
GATE_CREDIT = 8


def phys(k):
    return (k + KT // 2) % KT


def begun(tile):
    return tile + 1


def ds(start, size):
    return bass.ds(start, size)


def trunk(nc, x, norm1_g, norm2_g, mlp_w1, mlp_w2, final_g, a_w_in, a_ln_g, a_ws, a_bs, a_w_out, out):
    x_v = x.rearrange("a (m p) d -> p (a m) d", p=P)
    out_v = out.rearrange("a (m p) d -> p (a m) d", p=P)
    w_in_v = a_w_in.rearrange("a (k p) c -> p (a k) c", p=P)
    w_out_v = a_w_out.rearrange("a (e p) c -> p (a e) c", p=P)
    w1_v = mlp_w1.rearrange("a (k p) c -> p (a k) c", p=P)
    w2_v = mlp_w2.rearrange("a (f p) c -> p (a f) c", p=P)
    ws_v = a_ws.rearrange("a g t s -> t (a g) s")

    with ExitStack() as ctx:
        def sb(name, shape, dt=F32):
            return ctx.enter_context(nc.sbuf_tensor(name, shape, dt))

        def sem(name):
            return ctx.enter_context(nc.semaphore(name))

        ps = ctx.enter_context(nc.psum_tensor("banks", [P, BANKS, NB], F32))

        raw = sb("raw_weights", [P, PAIRS, 2, NB])
        w_high = sb("w_high", [P, RING, NB], F32R)
        w_low = sb("w_low", [P, RING, NB], F32R)
        act_high = sb("act_high", [P, KT, T], F32R)
        act_low = sb("act_low", [P, KT, T], F32R)
        rows = sb("rows", [P, MT, D])
        vn = rows[:, 0:MT // 2, :].rearrange("p (a c) (b j e) -> p (a c b) j e", c=1, b=2, j=JB)
        u = rows[:, MT // 2:MT, :]
        scratch = sb("scratch", [P, SCRATCH, NB])
        ws_nat = scratch[:, 0:2, :].rearrange("p a (g s) -> p (a g) s", s=P)
        ws_t = sb("ws_t", [P, GROUPS, P])
        bias = sb("bias", [P, GROUPS, P])
        final_b = ws_t.ap().rearrange("p g s -> p (g s)")
        ident = sb("ident", [P, P])
        gain_rows = sb("gain_rows", [2 * KT + JT, P])
        gains = sb("gains", [P, 2 * KT + JT])
        g1, g2, ln_g = gains[:, 0:KT], gains[:, KT:2 * KT], gains[:, 2 * KT:]
        x_sq = sb("x_sq", [P, MT])
        x_ms = sb("x_ms", [P, MT])
        x_rms = sb("x_rms", [P, MT])
        x_rstd = sb("x_rstd", [P, MT])
        ln_stats = sb("ln_stats", [P, MT, W // NB, 6])
        ln_mv = sb("ln_mv", [P, MT, 2])
        ln_ve = sb("ln_ve", [P, MT])
        ln_std = sb("ln_std", [P, MT])
        ln_rstd = sb("ln_rstd", [P, MT])
        y_sq = sb("y_sq", [P, MT])
        y_ms = sb("y_ms", [P, MT])
        y_r2 = sb("y_r2", [P, MT])
        o_sq = sb("o_sq", [P, MT])
        o_ms = sb("o_ms", [P, MT])
        o_rms = sb("o_rms", [P, MT])
        o_rstd = sb("o_rstd", [P, MT])
        with nc.sbuf_tensor("v_then_gated", [P, JT, MT, P], F32) as v:
            pass
        hid_high = sb("hid_high", [P, KT, T], F32R)
        hid_low = sb("hid_low", [P, KT, T], F32R)
        gated = v.ap().rearrange("p j m e -> p j (m e)")

        raw_landed = [sem(f"raw_landed{q}") for q in range(PAIRS)]
        x_landed = [sem(f"x_landed{m}") for m in range(MT)]
        gains_landed = sem("gains_landed")
        ws_landed = sem("ws_landed")
        bias_landed = sem("bias_landed")
        x_again = sem("x_again")
        final_landed = sem("final_landed")
        out_stored = sem("out_stored")
        w_high_done = sem("w_high_done")
        w_low_done = sem("w_low_done")
        tile_begun = sem("tile_begun")
        bank_full = sem("bank_full")
        act_read = sem("act_read")
        dve_read = sem("dve_read")
        ident_zero = sem("ident_zero")
        ident_done = sem("ident_done")
        ws_masked = sem("ws_masked")
        x_squared = sem("x_squared")
        x_meaned = sem("x_meaned")
        x_rooted = sem("x_rooted")
        x_inverted = sem("x_inverted")
        x_scaled = sem("x_scaled")
        ln_counted = sem("ln_counted")
        ln_step = sem("ln_step")
        ln_rooted = sem("ln_rooted")
        vn_done = sem("vn_done")
        gate_done = sem("gate_done")
        g_high_done = sem("g_high_done")
        g_low_done = sem("g_low_done")
        y_squared = sem("y_squared")
        y_step = sem("y_step")
        squared_done = sem("squared_done")
        hid_high_done = sem("hid_high_done")
        hid_low_done = sem("hid_low_done")
        o_half = sem("o_half")
        o_squared = sem("o_squared")
        o_meaned = sem("o_meaned")
        o_rooted = sem("o_rooted")
        o_inverted = sem("o_inverted")
        o_done = sem("o_done")

        block = ctx.enter_context(nc.Block())

        @block.sync
        def _(sp):
            def load_group(g, source, first):
                for q in range(PAIRS):
                    if not first:
                        sp.wait_ge(w_low_done, (g - 1) * 8 + (2 * q + 2))
                    sp.dma_start(raw[:, q], source(q)).then_inc(raw_landed[q], 16)

            for m in range(MT // 2):
                sp.dma_start(rows[:, m], x_v[:, m]).then_inc(x_landed[m], 16)
            load_group(0, lambda q: w_in_v[:, 2 * q:2 * q + 2, W:W + NB], True)
            for m in range(MT // 2, MT):
                sp.dma_start(rows[:, m], x_v[:, m]).then_inc(x_landed[m], 16)
            with sp.Fori(1, 4) as n:
                load_group(n, lambda q: w_in_v[:, 2 * q:2 * q + 2, ds(n * NB + W, NB)], False)
            with sp.Fori(0, 4) as b:
                load_group(b + G_U, lambda q: w_in_v[:, 2 * q:2 * q + 2, ds(b * NB, NB)], False)
            for n in range(2):
                for eh in range(2):
                    load_group(G_OUT + 2 * n + eh,
                               lambda q: w_out_v[:, 8 * eh + 2 * q:8 * eh + 2 * q + 2, n * NB:(n + 1) * NB], False)
                    if n == 0 and eh == 1:
                        sp.wait_ge(gate_done, GATE_CREDIT + 2 * JT)
                        sp.dma_start(rows[:, :, :], x_v).then_inc(x_again, 16)
                        sp.dma_start(final_b, final_g.rearrange("(a d) -> a d", a=1).to_broadcast([P, D]))\
                          .then_inc(final_landed, 16)
            with sp.Fori(0, MLP_BLOCKS) as b:
                with sp.Fori(0, 2) as s:
                    load_group(b * 4 + s + G_MLP,
                               lambda q: w1_v[:, 2 * q:2 * q + 2, ds(b * (8 * P) + s * NB, NB)], False)
                with sp.Fori(0, 2) as n:
                    load_group(b * 4 + n + (G_MLP + 2),
                               lambda q: w2_v[:, ds(b * 8 + 2 * q, 2), ds(n * NB, NB)], False)
            for m in range(MT):
                sp.wait_ge(o_done, m + 1)
                sp.dma_start(out_v[:, m], rows[:, m]).then_inc(out_stored, 16)
            sp.wait_ge(out_stored, 16 * MT)

        @block.gpsimd
        def _(pool):
            nc.gpsimd.memset(ident[:, :], 0.0).then_inc(ident_zero, 1)
            pool.wait_ge(ident_zero, 1)
            nc.gpsimd.affine_select(out=ident[:, :], in_=ident[:, :], compare_op=ALU.not_equal, fill=1.0,
                                    base=0, pattern=[[-1, P]], channel_multiplier=1).then_inc(ident_done, 1)
            pool.wait_ge(ws_landed, 16)
            nc.gpsimd.affine_select(out=ws_nat, in_=ws_nat, compare_op=ALU.is_ge, fill=0.0, base=0,
                                    pattern=[[0, GROUPS], [-1, P]], channel_multiplier=1).then_inc(ws_masked, 1)
            pool.sem_inc(gate_done, GATE_CREDIT)

            def split_low(tile, k):
                pool.wait_ge(w_high_done, tile + 1)
                nc.gpsimd.tensor_tensor(w_low[:, k % RING], raw[:, k // 2, k % 2],
                                        w_high[:, k % RING].bitcast(F32), ALU.subtract).then_inc(w_low_done, 1)

            for k in range(AHEAD):
                split_low(k, k)
            with pool.Fori(0, G_U) as g:
                for k in range(AHEAD, AHEAD + 8):
                    split_low(g * 8 + k, k % 8)
            with pool.Fori(0, 4) as b:
                for k in range(AHEAD, AHEAD + 8):
                    split_low(b * 8 + (8 * G_U + k), k % 8)
                for i in range(BANKS):
                    pool.wait_ge(dve_read, b * 8 + (DR_U + i + 1))
                    nc.gpsimd.tensor_tensor(gated[:, ds(b * JB + i // 2, 1), NB * (i % 2):NB * (i % 2 + 1)],
                                            scratch[:, i % SCRATCH:i % SCRATCH + 1, :],
                                            u[:, i // 2:i // 2 + 1, NB * (i % 2):NB * (i % 2 + 1)],
                                            ALU.mult).then_inc(gate_done, 1)
            with pool.Fori(G_OUT, N_GROUPS - 1) as g:
                for k in range(AHEAD, AHEAD + 8):
                    split_low(g * 8 + k, k % 8)
            for k in range(AHEAD, 8):
                split_low(8 * (N_GROUPS - 1) + k, k)

        @block.scalar
        def _(act):
            act.dma_start(gain_rows[0:KT, :], norm1_g.rearrange("a (k p) -> (a k) p", p=P)).then_inc(gains_landed, 16)
            act.dma_start(gain_rows[KT:2 * KT, :], norm2_g.rearrange("a (k p) -> (a k) p", p=P))\
               .then_inc(gains_landed, 16)
            act.dma_start(gain_rows[2 * KT:, :], a_ln_g.rearrange("a (k p) -> (a k) p", p=P)).then_inc(gains_landed, 16)
            act.dma_start(ws_nat, ws_v).then_inc(ws_landed, 16)
            act.dma_start(bias.ap().rearrange("p g t -> p (g t)"),
                          a_bs.rearrange("a g t -> a (g t)").to_broadcast([P, GROUPS * P])).then_inc(bias_landed, 16)

            def split_high(tile, landed, k, wait_slot=True):
                act.wait_ge(raw_landed[k // 2], landed)
                if wait_slot:
                    act.wait_ge(tile_begun, begun(tile - RING + 1))
                nc.scalar.activation(w_high[:, k % RING], raw[:, k // 2, k % 2], ACT.Copy).then_inc(w_high_done, 1)

            def split_high_group(g, steps=range(AHEAD, AHEAD + 8), between=None):
                for k in steps:
                    if between:
                        between(k - AHEAD)
                    split_high(g * 8 + k, g * 16 + 16 * (1 + k // 8), k % 8)

            def x_high(hf, k):
                act.wait_ge(bank_full, FILL_X + KT * hf + k + 1)
                nc.scalar.activation(act_high[:, k, NB * hf:NB * (hf + 1)], ps[:, k, :], ACT.Copy,
                                     scale=g1[:, k:k + 1]).then_inc(act_read, 1)

            act.wait_ge(dve_read, 1)
            for m in range(MT):
                act.wait_ge(x_landed[m], 16)
                nc.scalar.activation(gated[:, m, :], rows[:, m, :], ACT.Square,
                                     accum_out=x_sq[:, m:m + 1]).then_inc(x_squared, 1)
                act.wait_ge(x_meaned, m + 1)
                nc.scalar.activation(x_rms[:, m:m + 1], x_ms[:, m:m + 1], ACT.Sqrt).then_inc(x_rooted, 1)
                if m >= MT // 2:
                    for k in (2 * (m - MT // 2), 2 * (m - MT // 2) + 1):
                        x_high(0, k)
                if m == MT - 2:
                    split_high(0, 16, 0, wait_slot=False)
            for k in range(1, AHEAD):
                split_high(k, 16, k, wait_slot=False)
            for k in range(KT):
                x_high(1, k)
            split_high(AHEAD, 16, AHEAD, wait_slot=False)

            def gelu_v(n, m):
                act.wait_ge(bank_full, n * 8 + (FILL_V + m + 1))
                nc.scalar.activation(v[:, ds(n * JB, JB), m, :], ps[:, m, :].rearrange("p (j e) -> p j e", e=P),
                                     ACT.Gelu_apprx_tanh).then_inc(act_read, 1)

            act.wait_ge(x_squared, MT)
            split_high_group(0, range(AHEAD + 1, AHEAD + 8))
            for m in range(MT):
                gelu_v(0, m)
            with act.Fori(1, G_U) as n:
                split_high_group(n)
                for m in range(MT):
                    gelu_v(n, m)
            act.wait_ge(ln_step, MT + 1)
            nc.scalar.activation(ln_std[:, :], ln_ve[:, :], ACT.Sqrt).then_inc(ln_rooted, 1)

            with act.Fori(0, 4) as b:
                split_high_group(b + G_U)
                for i in range(BANKS):
                    act.wait_ge(bank_full, b * 16 + (FILL_U + i + 1))
                    act.wait_ge(gate_done, b * 8 + (i + 1))
                    nc.scalar.activation(u[:, i // 2, NB * (i % 2):NB * (i % 2 + 1)], ps[:, i, :],
                                         ACT.Gelu_apprx_tanh).then_inc(act_read, 1)

            def g_high(t):
                e = t % JT
                if t < JT:
                    act.wait_ge(gate_done, GATE_CREDIT + 2 * e + 2)
                if t >= RING:
                    act.wait_ge(tile_begun, begun(8 * G_OUT + t - RING + 1))
                nc.scalar.activation(act_high[:, t % RING, :], gated[:, e, :], ACT.Copy).then_inc(g_high_done, 1)

            def y_high(n, i):
                k = phys(n * JB + i % JB)
                act.wait_ge(bank_full, FILL_OUT + 16 * n + 8 + i + 1)
                nc.scalar.activation(act_high[:, k, NB * (i // JB):NB * (i // JB + 1)], ps[:, i, :], ACT.Copy,
                                     scale=g2[:, n * JB + i % JB:n * JB + i % JB + 1]).then_inc(act_read, 1)

            for t in range(AHEAD):
                g_high(t)
            for n in range(2):
                for eh in range(2):
                    def ahead(k):
                        t = JT * n + 8 * eh + k + AHEAD
                        if t < 2 * JT:
                            g_high(t)
                    split_high_group(G_OUT + 2 * n + eh, between=ahead)
                for i in range(BANKS):
                    y_high(n, i)
            for m in range(MT):
                nc.scalar.activation(gated[:, m, :], rows[:, m, :], ACT.Square,
                                     accum_out=y_sq[:, m:m + 1]).then_inc(y_squared, 1)

            def square(count, i):
                act.wait_ge(act_read, count + (AR_MLP + i + 1))
                nc.scalar.activation(scratch[:, i % SCRATCH], scratch[:, i % SCRATCH], ACT.Square)\
                  .then_inc(squared_done, 1)

            def mlp_block(b, last):
                with act.Fori(0, 2) as s:
                    split_high_group(b * 4 + s + G_MLP)
                    for i in range(BANKS):
                        act.wait_ge(bank_full, b * 32 + s * 8 + (FILL_MLP + i + 1))
                        act.wait_ge(hid_low_done, b * 16 + s * 8 + (i + 1))
                        nc.scalar.activation(scratch[:, i % SCRATCH], ps[:, i, :], ACT.Relu).then_inc(act_read, 1)
                        if i:
                            square(b * 16 + s * 8, i - 1)
                    square(b * 16 + s * 8, BANKS - 1)
                if last:
                    split_high_group(b * 4 + (G_MLP + 2))
                    split_high_group(b * 4 + (G_MLP + 3), range(AHEAD, 8))
                else:
                    with act.Fori(0, 2) as n:
                        split_high_group(b * 4 + n + (G_MLP + 2))

            with act.Fori(0, MLP_BLOCKS - 1) as b:
                mlp_block(b, False)
            mlp_block(MLP_BLOCKS - 1, True)

            for m in range(MT):
                act.wait_ge(dve_read, DR_MLP + 16 * MLP_BLOCKS - 8 + m + 1)
                nc.scalar.activation(act_high[:, m, :], rows[:, m, :], ACT.Square,
                                     accum_out=o_sq[:, m:m + 1]).then_inc(o_squared, 1)
                act.wait_ge(o_meaned, m + 1)
                nc.scalar.activation(o_rms[:, m:m + 1], o_ms[:, m:m + 1], ACT.Sqrt).then_inc(o_rooted, 1)

        @block.vector
        def _(dve):
            dve.wait_ge(bank_full, 1)
            nc.vector.tensor_copy(gains[:, :], ps[:, 7, 0:2 * KT + JT]).then_inc(dve_read, 1)
            dve.wait_ge(dve_read, 1)

            def rstd_step(m, squares, squared, ms, meaned, rms, rooted, rstd, inverted):
                c = slice(m, m + 1)
                dve.wait_ge(squared, m + 1)
                nc.vector.tensor_scalar(ms[:, c], squares[:, c], 1.0 / D, EPS, ALU.mult, ALU.add).then_inc(meaned, 1)
                dve.wait_ge(rooted, m + 1)
                nc.vector.reciprocal(rstd[:, c], rms[:, c]).then_inc(inverted, 1)
                dve.wait_ge(inverted, m + 1)

            def low_half(k, hf, bank, gain, full, high):
                dve.wait_ge(bank_full, full)
                dve.wait_ge(act_read, high)
                nc.vector.scalar_tensor_tensor(
                    out=act_low[:, k, NB * hf:NB * (hf + 1)], in0=ps[:, bank, :], scalar=gain,
                    in1=act_high[:, k, NB * hf:NB * (hf + 1)].bitcast(F32),
                    op0=ALU.mult, op1=ALU.subtract).then_inc(dve_read, 1)

            for m in range(MT):
                rstd_step(m, x_sq, x_squared, x_ms, x_meaned, x_rms, x_rooted, x_rstd, x_inverted)
                nc.vector.tensor_scalar(rows[:, m, :], rows[:, m, :], x_rstd[:, m:m + 1], None, ALU.mult)\
                  .then_inc(x_scaled, 1)
                if m >= MT // 2:
                    for k in (2 * (m - MT // 2), 2 * (m - MT // 2) + 1):
                        low_half(k, 0, k, g1[:, k:k + 1], FILL_X + k + 1, k + 1)
            for k in range(KT):
                low_half(k, 1, k, g1[:, k:k + 1], FILL_X + KT + k + 1, KT + k + 1)

            with dve.Fori(0, W // NB) as n:
                for m in range(MT):
                    dve.wait_ge(act_read, n * 8 + (AR_V + m + 1))
                    nc.vector.bn_stats(ln_stats[:, m, ds(n, 1), :], v[:, ds(n * JB, JB), m, :])\
                      .then_inc(ln_counted, 1)
            for i in range(2):
                dve.wait_ge(bank_full, FILL_WS + i + 1)
                nc.vector.tensor_copy(ws_t[:, 4 * i:4 * i + 4, :],
                                      ps[:, 6 + i, :].rearrange("p (g s) -> p g s", s=P)).then_inc(dve_read, 1)
            dve.wait_ge(ln_counted, MT * (W // NB))
            for m in range(MT):
                nc.vector.bn_aggr(ln_mv[:, m, :], ln_stats[:, m, :, :].rearrange("p a b -> p (a b)"))\
                  .then_inc(ln_step, 1)
            dve.wait_ge(ln_step, MT)
            nc.vector.tensor_scalar(ln_ve[:, :], ln_mv[:, :, 1], LN_EPS, None, ALU.add).then_inc(ln_step, 1)
            dve.wait_ge(ln_rooted, 1)
            nc.vector.reciprocal(ln_rstd[:, :], ln_std[:, :]).then_inc(ln_step, 1)
            dve.wait_ge(ln_step, MT + 2)
            dve.wait_ge(bias_landed, 16)

            with dve.Fori(0, 4) as b:
                dve.wait_ge(bank_full, b * 16 + FILL_U)
                for m in range(MT):
                    nc.vector.tensor_scalar(vn[:, m], v[:, ds(b * JB, JB), m, :], ln_mv[:, m, 0:1],
                                            ln_rstd[:, m:m + 1], ALU.subtract, ALU.mult).then_inc(vn_done, 1)
                for i in range(BANKS):
                    dve.wait_ge(bank_full, b * 16 + (FILL_U + 8 + i + 1))
                    dve.wait_ge(gate_done, b * 8 + (GATE_CREDIT + i + 1 - SCRATCH))
                    nc.vector.scalar_tensor_tensor(
                        out=scratch[:, i % SCRATCH, :].rearrange("p (c t) -> p c t", t=P),
                        in0=ps[:, i, :].rearrange("p (c t) -> p c t", t=P),
                        scalar=ln_g[:, ds(b * JB + i // 2, 1)],
                        in1=bias[:, ds(b * 2 + i // 4, 1), :].to_broadcast([P, JB, P]),
                        op0=ALU.mult, op1=ALU.add).then_inc(dve_read, 1)

            def g_low(t):
                e = t % JT
                dve.wait_ge(g_high_done, t + 1)
                nc.vector.tensor_tensor(act_low[:, t % RING, :], gated[:, e, :],
                                        act_high[:, t % RING, :].bitcast(F32), ALU.subtract).then_inc(g_low_done, 1)

            for t in range(AHEAD):
                g_low(t)
            for n in range(2):
                for t in range(JT * n + AHEAD, min(JT * (n + 1) + AHEAD, 2 * JT)):
                    g_low(t)
                if n == 0:
                    dve.wait_ge(x_again, 16)
                for m in range(MT):
                    dve.wait_ge(bank_full, FILL_OUT + 16 * n + m + 1)
                    nc.vector.tensor_tensor(rows[:, m, n * NB:(n + 1) * NB], ps[:, m, :],
                                            rows[:, m, n * NB:(n + 1) * NB], ALU.add).then_inc(dve_read, 1)
                for i in range(BANKS):
                    kk = n * JB + i % JB
                    low_half(phys(kk), i // JB, i, g2[:, kk:kk + 1],
                             FILL_OUT + 16 * n + 8 + i + 1, AR_OUT + 8 * n + i + 1)

            dve.wait_ge(y_squared, MT)
            nc.vector.tensor_scalar(y_ms[:, :], y_sq[:, :], 1.0 / D, EPS, ALU.mult, ALU.add).then_inc(y_step, 1)
            dve.wait_ge(y_step, 1)
            nc.vector.reciprocal(y_r2[:, :], y_ms[:, :]).then_inc(y_step, 1)
            dve.wait_ge(y_step, 2)
            dve.sem_inc(hid_low_done, SCRATCH)

            def hidden(j, i):
                return hid_high[:, ds(j, 1), NB * (i % 2):NB * (i % 2 + 1)], \
                    hid_low[:, ds(j, 1), NB * (i % 2):NB * (i % 2 + 1)]

            def hidden_low(count, j, i):
                high, low = hidden(j, i)
                dve.wait_ge(hid_high_done, count + (i + 1))
                nc.vector.tensor_tensor(low, scratch[:, i % SCRATCH:i % SCRATCH + 1, :], high.bitcast(F32),
                                        ALU.subtract).then_inc(hid_low_done, 1)

            with dve.Fori(0, MLP_BLOCKS) as b:
                with dve.Fori(0, 2) as s:
                    for i in range(BANKS):
                        dve.wait_ge(squared_done, b * 16 + s * 8 + (i + 1))
                        high, low = hidden(s * JB + i // 2, i)
                        nc.vector.tensor_copy(high, scratch[:, i % SCRATCH:i % SCRATCH + 1, :])\
                          .then_inc(hid_high_done, 1)
                        if i:
                            hidden_low(b * 16 + s * 8, s * JB + (i - 1) // 2, i - 1)
                    hidden_low(b * 16 + s * 8, s * JB + JB - 1, BANKS - 1)
                with dve.Fori(0, 2) as n:
                    dve.wait_ge(dve_read, b * 16 + n * 8 + (DR_MLP - 8))
                    for m in range(MT):
                        dve.wait_ge(bank_full, b * 32 + n * 8 + (FILL_MLP + 16 + m + 1))
                        nc.vector.scalar_tensor_tensor(
                            out=rows[:, m, ds(n * NB, NB)], in0=ps[:, m, :], scalar=y_r2[:, m:m + 1],
                            in1=rows[:, m, ds(n * NB, NB)], op0=ALU.mult, op1=ALU.add).then_inc(dve_read, 1)

            dve.wait_ge(final_landed, 16)
            for m in range(MT):
                rstd_step(m, o_sq, o_squared, o_ms, o_meaned, o_rms, o_rooted, o_rstd, o_inverted)
                nc.vector.scalar_tensor_tensor(out=rows[:, m, :], in0=rows[:, m, :], scalar=o_rstd[:, m:m + 1],
                                               in1=final_b, op0=ALU.mult, op1=ALU.mult).then_inc(o_done, 1)

        @block.tensor
        def _(pe):
            def products(bank, high, low, moving_high, moving_low, start, stop, first_of_tile):
                first = nc.tensor.matmul(ps[:, bank, :], high, moving_high, start=start, stop=False)
                if first_of_tile:
                    first.then_inc(tile_begun, 1)
                nc.tensor.matmul(ps[:, bank, :], high, moving_low, start=False, stop=False)
                last = nc.tensor.matmul(ps[:, bank, :], low, moving_high, start=False, stop=stop)
                if stop:
                    last.then_inc(bank_full, 1)

            def tokens_stationary(k, stat_high, stat_low, start, stop, free=None):
                for m in range(MT):
                    if free:
                        free(m)
                    c = slice(m * P, (m + 1) * P)
                    products(m, stat_high[:, c], stat_low[:, c], w_high[:, k % RING], w_low[:, k % RING],
                             start, stop, m == 0)

            def weights_stationary(k, mov_high, mov_low, start, stop, free=None):
                for i in range(BANKS):
                    if free:
                        free(i)
                    c = slice(i // 2 * P, (i // 2 + 1) * P)
                    h = slice(NB * (i % 2), NB * (i % 2 + 1))
                    products(i, w_high[:, k % RING, c], w_low[:, k % RING, c], mov_high[:, h], mov_low[:, h],
                             start, stop, i == 0)

            pe.wait_ge(ident_done, 1)
            pe.wait_ge(gains_landed, 48)
            n_gains = 2 * KT + JT
            nc.tensor.transpose(ps[:, 7, 0:n_gains], gain_rows[:, :], ident[0:n_gains, 0:n_gains])\
              .then_inc(bank_full, 1)

            for m in range(MT // 2):
                pe.wait_ge(x_scaled, m + 1)
                for k in range(KT):
                    if m == 0 and k == 7:
                        pe.wait_ge(dve_read, DR_X)
                    tr = nc.tensor.transpose(ps[:, k, m * P:(m + 1) * P], rows[:, m, k * P:(k + 1) * P], ident[:, :])
                    if m == MT // 2 - 1:
                        tr.then_inc(bank_full, 1)
            pe.wait_ge(x_scaled, MT)
            for k in range(KT):
                pe.wait_ge(dve_read, DR_X + k + 1)
                for c in range(MT // 2):
                    m = MT // 2 + c
                    tr = nc.tensor.transpose(ps[:, k, c * P:(c + 1) * P], rows[:, m, k * P:(k + 1) * P], ident[:, :])
                tr.then_inc(bank_full, 1)

            with pe.Fori(0, W // NB) as n:
                for k in range(KT):
                    pe.wait_ge(w_low_done, n * 8 + (k + 1))

                    def free(m):
                        pe.wait_ge(dve_read, DR_X + KT + m + 1)
                        pe.wait_ge(act_read, n * 8 + (AR_V - 7 + m))
                    pe.wait_ge(dve_read, DR_X + KT + k + 1)
                    tokens_stationary(k, act_high[:, k], act_low[:, k], k == 0, k == KT - 1, free if k == 0 else None)

            pe.wait_ge(ws_masked, 1)
            for i in range(2):
                pe.wait_ge(act_read, AR_U - 1 + i)
                for c in range(4):
                    tr = nc.tensor.transpose(ps[:, 6 + i, c * P:(c + 1) * P], ws_nat[:, 4 * i + c, :], ident[:, :])
                tr.then_inc(bank_full, 1)

            with pe.Fori(0, W // NB) as b:
                for k in range(KT):
                    pe.wait_ge(w_low_done, b * 8 + (8 * G_U + k + 1))

                    def free(i):
                        pe.wait_ge(act_read, b * 8 + (AR_U - 7 + i))
                        pe.wait_ge(dve_read, b * 8 + (DR_U - 7 + i))
                    weights_stationary(k, act_high[:, k], act_low[:, k], k == 0, k == KT - 1, free if k == 0 else None)
                pe.wait_ge(vn_done, b * 8 + 8)
                for i in range(BANKS):
                    pe.wait_ge(act_read, b * 8 + (AR_U + i + 1))
                    for c in range(4):
                        mm = nc.tensor.matmul(ps[:, i, c * P:(c + 1) * P], vn[:, 4 * (i % 2) + c, i // 2, :],
                                              ws_t[:, ds(b * 2 + i // 4, 1), :], start=True, stop=True)
                    mm.then_inc(bank_full, 1)

            for n in range(2):
                for e in range(JT):
                    t = JT * n + e
                    pe.wait_ge(w_low_done, 8 * G_OUT + t + 1)
                    pe.wait_ge(g_low_done, t + 1)

                    def free(m):
                        pe.wait_ge(dve_read, DR_OUT + 16 * n - 7 + m)
                    tokens_stationary(e, act_high[:, t % RING], act_low[:, t % RING], e == 0, e == JT - 1,
                                      free if e == 0 else None)
                for i in range(BANKS):
                    pe.wait_ge(dve_read, DR_OUT + 16 * n + (4 if i < 4 else 8))
                    for c in range(4):
                        kk = JB * n + i % JB
                        tr = nc.tensor.transpose(ps[:, i, c * P:(c + 1) * P],
                                                 rows[:, 4 * (i // JB) + c, kk * P:(kk + 1) * P], ident[:, :])
                    tr.then_inc(bank_full, 1)

            with pe.Fori(0, MLP_BLOCKS) as b:
                with pe.Fori(0, 2) as s:
                    for k in range(KT):
                        pe.wait_ge(w_low_done, b * 32 + s * 8 + (8 * G_MLP + k + 1))

                        def free(i):
                            pe.wait_ge(act_read, b * 16 + s * 8 + (AR_MLP - 7 + i))
                            pe.wait_ge(dve_read, b * 16 + (DR_MLP - 7 + i))
                        pe.wait_ge(dve_read, DR_OUT + 16 * (k // JB) + 8 + JB + k % JB + 1)
                        weights_stationary(k, act_high[:, phys(k)], act_low[:, phys(k)], k == 0, k == KT - 1,
                                           free if k == 0 else None)
                with pe.Fori(0, 2) as n:
                    for f in range(KT):
                        pe.wait_ge(w_low_done, b * 32 + n * 8 + (8 * G_MLP + 16 + f + 1))
                        pe.wait_ge(hid_low_done, b * 16 + (SCRATCH + 2 * f + 2))

                        def free(m):
                            pe.wait_ge(act_read, b * 16 + (AR_MLP + 8 + m + 1))
                            pe.wait_ge(dve_read, b * 16 + n * 8 + (DR_MLP - 7 + m))
                        tokens_stationary(f, hid_high[:, f], hid_low[:, f], f == 0, f == KT - 1,
                                          free if f == 0 else None)


_INS = ["x", "norm1_g", "norm2_g", "mlp_w1", "mlp_w2", "final_g", "a_w_in", "a_ln_g", "a_ws", "a_bs", "a_w_out"]


def kernel(**inputs):
    import numpy as _np
    import concourse.bacc as _bacc
    from concourse import mybir as _mybir
    from concourse.bass_utils import run_bass_kernel_spmd as _run

    nc = _bacc.Bacc("TRN2", target_bir_lowering=False, num_devices=1, dynamic_dma_scratch_size=4096)
    arrays, args = {}, []
    for name in _INS:
        a = _np.ascontiguousarray(inputs[name])
        arrays[f"in_{name}_dram"] = a
        args.append(nc.dram_tensor(f"in_{name}_dram", a.shape, _mybir.dt.from_np(a.dtype), kind="ExternalInput").ap())
    args.append(nc.dram_tensor("out_0_dram", (1, T, D), F32, kind="ExternalOutput").ap())
    trunk(nc, *args)
    r = _run(nc, [arrays], core_ids=[0])
    return r.results[0]["out_0_dram"]
```

```python
from contextlib import ExitStack

import concourse.bass as bass
from concourse import mybir

F32 = mybir.dt.float32
F32R = mybir.dt.float32r
ALU = mybir.AluOpType
ACT = mybir.ActivationFunctionType

P = 128
T = 1024
D = 1024
W = 2 * D
F = 4 * D
GROUPS = 8
NB = 512
MT = T // P
KT = D // P
JT = W // P
HALF = T // NB
BANKS = 8
JB = NB // P
WARM_UP = 4
RING = 4
AHEAD = RING - 1
PAIRS = 4
SCRATCH = 4
EPS = 1e-6
LN_EPS = 1e-5

G_V, G_U, G_OUT, G_MLP = 0, W // NB, 2 * W // NB, 2 * W // NB + 2 * D // NB
MLP_BLOCKS = F // (8 * P)
N_GROUPS = G_MLP + 4 * MLP_BLOCKS
TILES = 8 * N_GROUPS

FILL_X = 1
FILL_V = FILL_X + 2 * KT
FILL_WS = FILL_V + 8 * 4
FILL_U = FILL_WS + 2
FILL_OUT = FILL_U + 16 * 4
FILL_MLP = FILL_OUT + 16 * 2
AR_V = 2 * KT
AR_U = AR_V + 8 * 4
AR_OUT = AR_U + 8 * 4
AR_MLP = AR_OUT + 8 * 2
DR_X = 1
DR_V = DR_X + 2 * KT
DR_U = DR_V + 2
DR_OUT = DR_U + 8 * 4
DR_MLP = DR_OUT + 16 * 2
GATE_CREDIT = 8


def phys(k):
    return (k + KT // 2) % KT


def begun(tile):
    return tile + 1


def ds(start, size):
    return bass.ds(start, size)


def trunk(nc, x, norm1_g, norm2_g, mlp_w1, mlp_w2, final_g, a_w_in, a_ln_g, a_ws, a_bs, a_w_out, out):
    x_v = x.rearrange("a (m p) d -> p (a m) d", p=P)
    out_v = out.rearrange("a (m p) d -> p (a m) d", p=P)
    w_in_v = a_w_in.rearrange("a (k p) c -> p (a k) c", p=P)
    w_out_v = a_w_out.rearrange("a (e p) c -> p (a e) c", p=P)
    w1_v = mlp_w1.rearrange("a (k p) c -> p (a k) c", p=P)
    w2_v = mlp_w2.rearrange("a (f p) c -> p (a f) c", p=P)
    ws_v = a_ws.rearrange("a g t s -> t (a g) s")

    with ExitStack() as ctx:
        def sb(name, shape, dt=F32):
            return ctx.enter_context(nc.sbuf_tensor(name, shape, dt))

        def sem(name):
            return ctx.enter_context(nc.semaphore(name))

        ps = ctx.enter_context(nc.psum_tensor("banks", [P, BANKS, NB], F32))

        raw = sb("raw_weights", [P, PAIRS, 2, NB])
        w_high = sb("w_high", [P, RING, NB], F32R)
        w_low = sb("w_low", [P, RING, NB], F32R)
        act_high = sb("act_high", [P, KT, T], F32R)
        act_low = sb("act_low", [P, KT, T], F32R)
        rows = sb("rows", [P, MT, D])
        vn = rows[:, 0:MT // 2, :].rearrange("p (a c) (b j e) -> p (a c b) j e", c=1, b=2, j=JB)
        u = rows[:, MT // 2:MT, :]
        scratch = sb("scratch", [P, SCRATCH, NB])
        ws_nat = scratch[:, 0:2, :].rearrange("p a (g s) -> p (a g) s", s=P)
        ws_t = sb("ws_t", [P, GROUPS, P])
        bias = sb("bias", [P, GROUPS, P])
        final_b = ws_t.ap().rearrange("p g s -> p (g s)")
        ident = sb("ident", [P, P])
        gain_rows = sb("gain_rows", [2 * KT + JT, P])
        gains = sb("gains", [P, 2 * KT + JT])
        g1, g2, ln_g = gains[:, 0:KT], gains[:, KT:2 * KT], gains[:, 2 * KT:]
        table_load = sb("table_load", [P, 1])
        x_sq = sb("x_sq", [P, MT])
        x_ms = sb("x_ms", [P, MT])
        x_rms = sb("x_rms", [P, MT])
        x_rstd = sb("x_rstd", [P, MT])
        ln_stats = sb("ln_stats", [P, MT, W // NB, 6])
        ln_mv = sb("ln_mv", [P, MT, 2])
        ln_ve = sb("ln_ve", [P, MT])
        ln_std = sb("ln_std", [P, MT])
        ln_rstd = sb("ln_rstd", [P, MT])
        y_sq = sb("y_sq", [P, MT])
        y_ms = sb("y_ms", [P, MT])
        y_r2 = sb("y_r2", [P, MT])
        o_sq_a = sb("o_sq_a", [P, MT])
        o_sq_b = sb("o_sq_b", [P, MT])
        o_ms_a = sb("o_ms_a", [P, MT])
        o_ms = sb("o_ms", [P, MT])
        o_rms = sb("o_rms", [P, MT])
        o_rstd = sb("o_rstd", [P, MT])
        with nc.sbuf_tensor("v_then_gated", [P, JT, MT, P], F32) as v:
            pass
        hid_high = sb("hid_high", [P, KT, T], F32R)
        hid_low = sb("hid_low", [P, KT, T], F32R)
        gated = v.ap().rearrange("p j m e -> p j (m e)")

        def last_w(k):
            return act_high[:, k, 0:NB], act_low[:, k, 0:NB]

        raw_landed = [sem(f"raw_landed{q}") for q in range(PAIRS)]
        x_landed = [sem(f"x_landed{m}") for m in range(MT)]
        gains_landed = sem("gains_landed")
        ws_landed = sem("ws_landed")
        bias_landed = sem("bias_landed")
        x_again = sem("x_again")
        final_landed = sem("final_landed")
        out_stored = sem("out_stored")
        w_high_done = sem("w_high_done")
        w_low_done = sem("w_low_done")
        tile_begun = sem("tile_begun")
        bank_full = sem("bank_full")
        act_read = sem("act_read")
        dve_read = sem("dve_read")
        ident_zero = sem("ident_zero")
        ident_done = sem("ident_done")
        ws_masked = sem("ws_masked")
        x_squared = sem("x_squared")
        x_meaned = sem("x_meaned")
        x_rooted = sem("x_rooted")
        x_inverted = sem("x_inverted")
        x_scaled = sem("x_scaled")
        ln_counted = sem("ln_counted")
        ln_step = sem("ln_step")
        ln_rooted = sem("ln_rooted")
        vn_done = sem("vn_done")
        gate_done = sem("gate_done")
        g_high_done = sem("g_high_done")
        g_low_done = sem("g_low_done")
        y_squared = sem("y_squared")
        y_step = sem("y_step")
        squared_done = sem("squared_done")
        hid_high_done = sem("hid_high_done")
        hid_low_done = sem("hid_low_done")
        o_half = sem("o_half")
        o_squared = sem("o_squared")
        o_meaned = sem("o_meaned")
        o_rooted = sem("o_rooted")
        o_inverted = sem("o_inverted")
        o_done = sem("o_done")

        block = ctx.enter_context(nc.Block())

        @block.sync
        def _(sp):
            def load_group(g, source):
                for q in range(PAIRS):
                    sp.wait_ge(w_low_done, g * 8 + (2 * q + 2 - 8))
                    sp.dma_start(raw[:, q], source(q)).then_inc(raw_landed[q], 16)

            for m in range(MT):
                sp.dma_start(rows[:, m], x_v[:, m]).then_inc(x_landed[m], 16)
                if m == MT // 2 - 1:
                    sp.dma_start(raw[:, 0], w_in_v[:, 0:2, W:W + NB]).then_inc(raw_landed[0], 16)
            for q in range(1, PAIRS):
                sp.dma_start(raw[:, q], w_in_v[:, 2 * q:2 * q + 2, W:W + NB]).then_inc(raw_landed[q], 16)
            sp.dma_start(ws_nat, ws_v).then_inc(ws_landed, 16)
            sp.dma_start(bias.ap().rearrange("p g t -> p (g t)"),
                         a_bs.rearrange("a g t -> a (g t)").to_broadcast([P, GROUPS * P])).then_inc(bias_landed, 16)
            with sp.Fori(1, 4) as n:
                load_group(n, lambda q: w_in_v[:, 2 * q:2 * q + 2, ds(n * NB + W, NB)])
            with sp.Fori(0, 4) as b:
                load_group(b + G_U, lambda q: w_in_v[:, 2 * q:2 * q + 2, ds(b * NB, NB)])
            for n in range(2):
                for eh in range(2):
                    load_group(G_OUT + 2 * n + eh,
                               lambda q: w_out_v[:, 8 * eh + 2 * q:8 * eh + 2 * q + 2, n * NB:(n + 1) * NB])
                    if n == 0 and eh == 1:
                        sp.wait_ge(gate_done, GATE_CREDIT + 2 * JT)
                        sp.dma_start(rows[:, :, :], x_v).then_inc(x_again, 16)
                        sp.dma_start(final_b, final_g.rearrange("(a d) -> a d", a=1).to_broadcast([P, D]))\
                          .then_inc(final_landed, 16)
            with sp.Fori(0, MLP_BLOCKS) as b:
                with sp.Fori(0, 2) as s:
                    load_group(b * 4 + s + G_MLP,
                               lambda q: w1_v[:, 2 * q:2 * q + 2, ds(b * (8 * P) + s * NB, NB)])
                with sp.Fori(0, 2) as n:
                    load_group(b * 4 + n + (G_MLP + 2),
                               lambda q: w2_v[:, ds(b * 8 + 2 * q, 2), ds(n * NB, NB)])
            for m in range(MT - 1):
                sp.wait_ge(o_done, m + 1)
                sp.dma_start(out_v[:, m], rows[:, m]).then_inc(out_stored, 16)
            for h in range(2):
                sp.wait_ge(o_done, MT + h)
                sp.dma_start(out_v[:, MT - 1, NB * h:NB * (h + 1)], rows[:, MT - 1, NB * h:NB * (h + 1)])\
                  .then_inc(out_stored, 16)
            sp.wait_ge(out_stored, 16 * (MT + 1))

        @block.gpsimd
        def _(pool):
            nc.gpsimd.memset(ident[:, :], 0.0).then_inc(ident_zero, 1)
            pool.wait_ge(ident_zero, 1)
            nc.gpsimd.affine_select(out=ident[:, :], in_=ident[:, :], compare_op=ALU.not_equal, fill=1.0,
                                    base=0, pattern=[[-1, P]], channel_multiplier=1).then_inc(ident_done, 1)
            pool.sem_inc(gate_done, GATE_CREDIT)

            def split_low(tile, k, last=False):
                high, low = last_w(k) if last else (w_high[:, k % RING], w_low[:, k % RING])
                pool.wait_ge(w_high_done, tile + 1)
                nc.gpsimd.tensor_tensor(low, raw[:, k // 2, k % 2], high.bitcast(F32), ALU.subtract)\
                  .then_inc(w_low_done, 1)

            for k in range(AHEAD):
                split_low(k, k)
            with pool.Fori(0, G_U - 1) as g:
                for k in range(AHEAD, AHEAD + 8):
                    split_low(g * 8 + k, k % 8)
            pool.wait_ge(ws_landed, 16)
            nc.gpsimd.affine_select(out=ws_nat, in_=ws_nat, compare_op=ALU.is_ge, fill=0.0, base=0,
                                    pattern=[[0, GROUPS], [-1, P]], channel_multiplier=1).then_inc(ws_masked, 1)
            for k in range(AHEAD, AHEAD + 8):
                split_low((G_U - 1) * 8 + k, k % 8)
            with pool.Fori(0, 4) as b:
                for k in range(AHEAD, AHEAD + 8):
                    split_low(b * 8 + (8 * G_U + k), k % 8)
                for i in range(BANKS):
                    pool.wait_ge(dve_read, b * 8 + (DR_U + i + 1))
                    nc.gpsimd.tensor_tensor(gated[:, ds(b * JB + i // 2, 1), NB * (i % 2):NB * (i % 2 + 1)],
                                            scratch[:, i % SCRATCH:i % SCRATCH + 1, :],
                                            u[:, i // 2:i // 2 + 1, NB * (i % 2):NB * (i % 2 + 1)],
                                            ALU.mult).then_inc(gate_done, 1)
            with pool.Fori(G_OUT, N_GROUPS - 2) as g:
                for k in range(AHEAD, AHEAD + 8):
                    split_low(g * 8 + k, k % 8)
            for k in range(AHEAD, 8):
                split_low(8 * (N_GROUPS - 2) + k, k)
            for k in range(8):
                split_low(8 * (N_GROUPS - 1) + k, k, last=True)

        @block.scalar
        def _(act):
            act.dma_start(gain_rows[0:KT, :], norm1_g.rearrange("a (k p) -> (a k) p", p=P)).then_inc(gains_landed, 16)
            act.dma_start(gain_rows[KT:2 * KT, :], norm2_g.rearrange("a (k p) -> (a k) p", p=P))\
               .then_inc(gains_landed, 16)
            act.dma_start(gain_rows[2 * KT:, :], a_ln_g.rearrange("a (k p) -> (a k) p", p=P)).then_inc(gains_landed, 16)

            def split_high(tile, landed, k, wait_slot=True, last=False):
                high = last_w(k)[0] if last else w_high[:, k % RING]
                act.wait_ge(raw_landed[k // 2], landed)
                if wait_slot:
                    act.wait_ge(tile_begun, begun(tile - RING + 1))
                nc.scalar.activation(high, raw[:, k // 2, k % 2], ACT.Copy).then_inc(w_high_done, 1)

            def split_high_group(g, steps=range(AHEAD, AHEAD + 8), between=None):
                for k in steps:
                    if between:
                        between(k - AHEAD)
                    split_high(g * 8 + k, g * 16 + 16 * (1 + k // 8), k % 8)

            def x_high(hf, k):
                act.wait_ge(bank_full, FILL_X + KT * hf + k + 1)
                nc.scalar.activation(act_high[:, k, NB * hf:NB * (hf + 1)], ps[:, k if hf == 0 else 4 + k % 4, :], ACT.Copy,
                                     scale=g1[:, k:k + 1]).then_inc(act_read, 1)

            def square_x(m):
                act.wait_ge(x_landed[m], 16)
                nc.scalar.activation(gated[:, m, :], rows[:, m, :], ACT.Square,
                                     accum_out=x_sq[:, m:m + 1]).then_inc(x_squared, 1)

            def root_x(m):
                act.wait_ge(x_meaned, m + 1)
                nc.scalar.activation(x_rms[:, m:m + 1], x_ms[:, m:m + 1], ACT.Sqrt).then_inc(x_rooted, 1)

            act.wait_ge(ident_done, 1)
            nc.scalar.activation(table_load[:, :], ident[:, 0:1], ACT.Sqrt)
            square_x(0)
            for m in range(1, MT // 2):
                square_x(m)
                root_x(m - 1)
            root_x(MT // 2 - 1)
            split_high(0, 16, 0, wait_slot=False)
            square_x(4)
            act.wait_ge(dve_read, DR_X)
            for k in range(KT):
                x_high(0, k)
                if k == 3:
                    split_high(1, 16, 1, wait_slot=False)
                if 3 <= k < 7:
                    root_x(k + 1)
                if 3 <= k < 6:
                    square_x(k + 2)
                if k == 4 or k == 7:
                    t = 2 if k == 4 else 3
                    split_high(t, 16, t, wait_slot=False)
            for k in range(KT):
                x_high(1, k)

            def gelu_v(n, m):
                act.wait_ge(bank_full, n * 8 + (FILL_V + m + 1))
                nc.scalar.activation(v[:, ds(n * JB, JB), m, :], ps[:, m, :].rearrange("p (j e) -> p j e", e=P),
                                     ACT.Gelu_apprx_tanh).then_inc(act_read, 1)

            act.wait_ge(x_squared, MT)
            split_high_group(0, range(AHEAD + 1, AHEAD + 8))
            for m in range(MT):
                gelu_v(0, m)
            with act.Fori(1, G_U) as n:
                split_high_group(n)
                for m in range(MT):
                    gelu_v(n, m)
            act.wait_ge(ln_step, MT + 1)
            nc.scalar.activation(ln_std[:, :], ln_ve[:, :], ACT.Sqrt).then_inc(ln_rooted, 1)

            with act.Fori(0, 4) as b:
                split_high_group(b + G_U)
                for i in range(BANKS):
                    act.wait_ge(bank_full, b * 16 + (FILL_U + i + 1))
                    act.wait_ge(gate_done, b * 8 + (i + 1))
                    nc.scalar.activation(u[:, i // 2, NB * (i % 2):NB * (i % 2 + 1)], ps[:, i, :],
                                         ACT.Gelu_apprx_tanh).then_inc(act_read, 1)

            def g_high(t):
                e = t % JT
                if t < JT:
                    act.wait_ge(gate_done, GATE_CREDIT + 2 * e + 2)
                if t >= RING:
                    act.wait_ge(tile_begun, begun(8 * G_OUT + t - RING + 1))
                nc.scalar.activation(act_high[:, t % RING, :], gated[:, e, :], ACT.Copy).then_inc(g_high_done, 1)

            def y_high(n, i):
                k = phys(n * JB + i % JB)
                act.wait_ge(bank_full, FILL_OUT + 16 * n + 8 + i + 1)
                nc.scalar.activation(act_high[:, k, NB * (i // JB):NB * (i // JB + 1)], ps[:, i, :], ACT.Copy,
                                     scale=g2[:, n * JB + i % JB:n * JB + i % JB + 1]).then_inc(act_read, 1)

            for t in range(AHEAD):
                g_high(t)
            for n in range(2):
                for eh in range(2):
                    def ahead(k):
                        t = JT * n + 8 * eh + k + AHEAD
                        if t < 2 * JT:
                            g_high(t)
                    split_high_group(G_OUT + 2 * n + eh, between=ahead)
                for i in range(BANKS):
                    y_high(n, i)
            for m in range(MT):
                nc.scalar.activation(gated[:, m, :], rows[:, m, :], ACT.Square,
                                     accum_out=y_sq[:, m:m + 1]).then_inc(y_squared, 1)

            def square(count, i):
                act.wait_ge(act_read, count + (AR_MLP + i + 1))
                nc.scalar.activation(scratch[:, i % SCRATCH], scratch[:, i % SCRATCH], ACT.Square)\
                  .then_inc(squared_done, 1)

            def mlp_block(b, last):
                with act.Fori(0, 2) as s:
                    split_high_group(b * 4 + s + G_MLP)
                    for i in range(BANKS):
                        act.wait_ge(bank_full, b * 32 + s * 8 + (FILL_MLP + i + 1))
                        act.wait_ge(hid_low_done, b * 16 + s * 8 + (i + 1))
                        nc.scalar.activation(scratch[:, i % SCRATCH], ps[:, i, :], ACT.Relu).then_inc(act_read, 1)
                        if i:
                            square(b * 16 + s * 8, i - 1)
                    square(b * 16 + s * 8, BANKS - 1)
                if last:
                    split_high_group(N_GROUPS - 2, range(AHEAD, 8))
                    act.wait_ge(tile_begun, begun(8 * (N_GROUPS - 2)))
                    for k in range(8):
                        split_high(8 * (N_GROUPS - 1) + k, 16 * N_GROUPS, k, wait_slot=False, last=True)
                else:
                    with act.Fori(0, 2) as n:
                        split_high_group(b * 4 + n + (G_MLP + 2))

            with act.Fori(0, MLP_BLOCKS - 1) as b:
                mlp_block(b, False)
            mlp_block(MLP_BLOCKS - 1, True)

            for m in range(MT):
                act.wait_ge(dve_read, DR_MLP + 16 * MLP_BLOCKS - 16 + m + 1)
                nc.scalar.activation(act_low[:, m, NB:], rows[:, m, 0:NB], ACT.Square,
                                     accum_out=o_sq_a[:, m:m + 1]).then_inc(o_half, 1)
            for m in range(MT):
                act.wait_ge(dve_read, DR_MLP + 16 * MLP_BLOCKS - 8 + m + 1)
                nc.scalar.activation(act_high[:, m, NB:], rows[:, m, NB:], ACT.Square,
                                     accum_out=o_sq_b[:, m:m + 1]).then_inc(o_squared, 1)
                act.wait_ge(o_meaned, m + 1)
                nc.scalar.activation(o_rms[:, m:m + 1], o_ms[:, m:m + 1], ACT.Sqrt).then_inc(o_rooted, 1)

        @block.vector
        def _(dve):
            def low_half(k, hf, bank, gain, full, high):
                dve.wait_ge(bank_full, full)
                dve.wait_ge(act_read, high)
                nc.vector.scalar_tensor_tensor(
                    out=act_low[:, k, NB * hf:NB * (hf + 1)], in0=ps[:, bank, :], scalar=gain,
                    in1=act_high[:, k, NB * hf:NB * (hf + 1)].bitcast(F32),
                    op0=ALU.mult, op1=ALU.subtract).then_inc(dve_read, 1)

            def mean_x(m):
                c = slice(m, m + 1)
                dve.wait_ge(x_squared, m + 1)
                nc.vector.tensor_scalar(x_ms[:, c], x_sq[:, c], 1.0 / D, EPS, ALU.mult, ALU.add)\
                  .then_inc(x_meaned, 1)

            def scale_x(m):
                c = slice(m, m + 1)
                dve.wait_ge(x_rooted, m + 1)
                nc.vector.reciprocal(x_rstd[:, c], x_rms[:, c]).then_inc(x_inverted, 1)
                dve.wait_ge(x_inverted, m + 1)
                nc.vector.tensor_scalar(rows[:, m, :], rows[:, m, :], x_rstd[:, c], None, ALU.mult)\
                  .then_inc(x_scaled, 1)

            mean_x(0)
            for m in range(1, MT // 2):
                mean_x(m)
                scale_x(m - 1)
                if m == 1:
                    dve.wait_ge(bank_full, 1)
                    nc.vector.tensor_copy(gains[:, :], ps[:, 7, 0:2 * KT + JT]).then_inc(dve_read, 1)
            scale_x(MT // 2 - 1)
            mean_x(4)
            dve.wait_ge(dve_read, DR_X)
            for hf in range(2):
                for k in range(KT):
                    low_half(k, hf, k if hf == 0 else 4 + k % 4, g1[:, k:k + 1],
                             FILL_X + KT * hf + k + 1, KT * hf + k + 1)
                    if hf == 0 and 3 <= k < 7:
                        scale_x(k + 1)
                    if hf == 0 and 3 <= k < 6:
                        mean_x(k + 2)

            with dve.Fori(0, W // NB) as n:
                for m in range(MT):
                    dve.wait_ge(act_read, n * 8 + (AR_V + m + 1))
                    nc.vector.bn_stats(ln_stats[:, m, ds(n, 1), :], v[:, ds(n * JB, JB), m, :])\
                      .then_inc(ln_counted, 1)
            for i in range(2):
                dve.wait_ge(bank_full, FILL_WS + i + 1)
                nc.vector.tensor_copy(ws_t[:, 4 * i:4 * i + 4, :],
                                      ps[:, 6 + i, :].rearrange("p (g s) -> p g s", s=P)).then_inc(dve_read, 1)
            dve.wait_ge(ln_counted, MT * (W // NB))
            for m in range(MT):
                nc.vector.bn_aggr(ln_mv[:, m, :], ln_stats[:, m, :, :].rearrange("p a b -> p (a b)"))\
                  .then_inc(ln_step, 1)
            dve.wait_ge(ln_step, MT)
            nc.vector.tensor_scalar(ln_ve[:, :], ln_mv[:, :, 1], LN_EPS, None, ALU.add).then_inc(ln_step, 1)
            dve.wait_ge(ln_rooted, 1)
            nc.vector.reciprocal(ln_rstd[:, :], ln_std[:, :]).then_inc(ln_step, 1)
            dve.wait_ge(ln_step, MT + 2)
            dve.wait_ge(bias_landed, 16)

            def g_low(t):
                e = t % JT
                dve.wait_ge(g_high_done, t + 1)
                nc.vector.tensor_tensor(act_low[:, t % RING, :], gated[:, e, :],
                                        act_high[:, t % RING, :].bitcast(F32), ALU.subtract).then_inc(g_low_done, 1)

            def gating_block(b, last=False):
                dve.wait_ge(bank_full, b * 16 + FILL_U)
                for m in range(MT):
                    nc.vector.tensor_scalar(vn[:, m], v[:, ds(b * JB, JB), m, :], ln_mv[:, m, 0:1],
                                            ln_rstd[:, m:m + 1], ALU.subtract, ALU.mult).then_inc(vn_done, 1)
                for i in range(BANKS):
                    dve.wait_ge(bank_full, b * 16 + (FILL_U + 8 + i + 1))
                    dve.wait_ge(gate_done, b * 8 + (GATE_CREDIT + i + 1 - SCRATCH))
                    nc.vector.scalar_tensor_tensor(
                        out=scratch[:, i % SCRATCH, :].rearrange("p (c t) -> p c t", t=P),
                        in0=ps[:, i, :].rearrange("p (c t) -> p c t", t=P),
                        scalar=ln_g[:, ds(b * JB + i // 2, 1)],
                        in1=bias[:, ds(b * 2 + i // 4, 1), :].to_broadcast([P, JB, P]),
                        op0=ALU.mult, op1=ALU.add).then_inc(dve_read, 1)
                    if last and i == 5:
                        g_low(0)

            with dve.Fori(0, W // NB - 1) as b:
                gating_block(b)
            gating_block(W // NB - 1, last=True)
            for t in range(1, AHEAD):
                g_low(t)
            for n in range(2):
                for t in range(JT * n + AHEAD, min(JT * (n + 1) + AHEAD, 2 * JT)):
                    g_low(t)
                if n == 0:
                    dve.wait_ge(x_again, 16)
                for m in range(MT):
                    dve.wait_ge(bank_full, FILL_OUT + 16 * n + m + 1)
                    nc.vector.tensor_tensor(rows[:, m, n * NB:(n + 1) * NB], ps[:, m, :],
                                            rows[:, m, n * NB:(n + 1) * NB], ALU.add).then_inc(dve_read, 1)
                for i in range(BANKS):
                    kk = n * JB + i % JB
                    low_half(phys(kk), i // JB, i, g2[:, kk:kk + 1],
                             FILL_OUT + 16 * n + 8 + i + 1, AR_OUT + 8 * n + i + 1)

            dve.wait_ge(y_squared, MT)
            nc.vector.tensor_scalar(y_ms[:, :], y_sq[:, :], 1.0 / D, EPS, ALU.mult, ALU.add).then_inc(y_step, 1)
            dve.wait_ge(y_step, 1)
            nc.vector.reciprocal(y_r2[:, :], y_ms[:, :]).then_inc(y_step, 1)
            dve.wait_ge(y_step, 2)
            dve.sem_inc(hid_low_done, SCRATCH)

            def hidden(j, i):
                return hid_high[:, ds(j, 1), NB * (i % 2):NB * (i % 2 + 1)], \
                    hid_low[:, ds(j, 1), NB * (i % 2):NB * (i % 2 + 1)]

            def hidden_low(count, j, i):
                high, low = hidden(j, i)
                dve.wait_ge(hid_high_done, count + (i + 1))
                nc.vector.tensor_tensor(low, scratch[:, i % SCRATCH:i % SCRATCH + 1, :], high.bitcast(F32),
                                        ALU.subtract).then_inc(hid_low_done, 1)

            def add_tile(b, n, m):
                dve.wait_ge(bank_full, b * 32 + n * 8 + (FILL_MLP + 16 + m + 1))
                nc.vector.scalar_tensor_tensor(
                    out=rows[:, m, ds(n * NB, NB)], in0=ps[:, m, :], scalar=y_r2[:, m:m + 1],
                    in1=rows[:, m, ds(n * NB, NB)], op0=ALU.mult, op1=ALU.add).then_inc(dve_read, 1)

            def add_output(b, n):
                dve.wait_ge(dve_read, b * 16 + n * 8 + (DR_MLP - 8))
                for m in range(MT):
                    add_tile(b, n, m)

            def mlp_block(b, last=False):
                with dve.Fori(0, 2) as s:
                    for i in range(BANKS):
                        dve.wait_ge(squared_done, b * 16 + s * 8 + (i + 1))
                        high, low = hidden(s * JB + i // 2, i)
                        nc.vector.tensor_copy(high, scratch[:, i % SCRATCH:i % SCRATCH + 1, :])\
                          .then_inc(hid_high_done, 1)
                        if i:
                            hidden_low(b * 16 + s * 8, s * JB + (i - 1) // 2, i - 1)
                    hidden_low(b * 16 + s * 8, s * JB + JB - 1, BANKS - 1)
                if last:
                    add_output(b, 0)
                else:
                    with dve.Fori(0, 2) as n:
                        add_output(b, n)

            with dve.Fori(0, MLP_BLOCKS - 1) as b:
                mlp_block(b)
            mlp_block(MLP_BLOCKS - 1, last=True)

            dve.wait_ge(o_half, MT)
            nc.vector.tensor_scalar(o_ms_a[:, :], o_sq_a[:, :], 1.0 / D, EPS, ALU.mult, ALU.add).then_inc(y_step, 1)
            dve.wait_ge(y_step, 3)
            dve.wait_ge(final_landed, 16)
            dve.wait_ge(dve_read, DR_MLP + 16 * MLP_BLOCKS - 8)
            for m in range(MT):
                c = slice(m, m + 1)
                add_tile(MLP_BLOCKS - 1, 1, m)
                dve.wait_ge(o_squared, m + 1)
                nc.vector.scalar_tensor_tensor(out=o_ms[:, c], in0=o_sq_b[:, c], scalar=1.0 / D, in1=o_ms_a[:, c],
                                               op0=ALU.mult, op1=ALU.add).then_inc(o_meaned, 1)
                dve.wait_ge(o_rooted, m + 1)
                nc.vector.reciprocal(o_rstd[:, c], o_rms[:, c]).then_inc(o_inverted, 1)
                dve.wait_ge(o_inverted, m + 1)
                for h in [slice(0, D)] if m < MT - 1 else [slice(0, NB), slice(NB, D)]:
                    nc.vector.scalar_tensor_tensor(out=rows[:, m, h], in0=rows[:, m, h], scalar=o_rstd[:, c],
                                                   in1=final_b[:, h], op0=ALU.mult, op1=ALU.mult).then_inc(o_done, 1)

        @block.tensor
        def _(pe):
            def products(bank, high, low, moving_high, moving_low, start, stop, first_of_tile):
                first = nc.tensor.matmul(ps[:, bank, :], high, moving_high, start=start, stop=False)
                if first_of_tile:
                    first.then_inc(tile_begun, 1)
                nc.tensor.matmul(ps[:, bank, :], high, moving_low, start=False, stop=False)
                last = nc.tensor.matmul(ps[:, bank, :], low, moving_high, start=False, stop=stop)
                if stop:
                    last.then_inc(bank_full, 1)

            def tokens_stationary(k, stat_high, stat_low, start, stop, free=None, tiles=range(MT), first=0):
                for m in tiles:
                    if free:
                        free(m)
                    c = slice(m * P, (m + 1) * P)
                    products(m, stat_high[:, c], stat_low[:, c], w_high[:, k % RING], w_low[:, k % RING],
                             start, stop, m == first)

            def weights_stationary(k, mov_high, mov_low, start, stop, free=None):
                for i in range(BANKS):
                    if free:
                        free(i)
                    c = slice(i // 2 * P, (i // 2 + 1) * P)
                    h = slice(NB * (i % 2), NB * (i % 2 + 1))
                    products(i, w_high[:, k % RING, c], w_low[:, k % RING, c], mov_high[:, h], mov_low[:, h],
                             start, stop, i == 0)

            pe.wait_ge(ident_done, 1)
            with pe.Fori(0, WARM_UP):
                for _ in range(4):
                    nc.tensor.matmul(ps[:, 0, 0:P], ident[:, :], ident[:, :], start=True, stop=True)

            pe.wait_ge(gains_landed, 48)
            n_gains = 2 * KT + JT
            nc.tensor.transpose(ps[:, 7, 0:n_gains], gain_rows[:, :], ident[0:n_gains, 0:n_gains])\
              .then_inc(bank_full, 1)

            for m in range(MT // 2):
                pe.wait_ge(x_scaled, m + 1)
                for k in range(KT):
                    if m == 0 and k == 7:
                        pe.wait_ge(dve_read, DR_X)
                    tr = nc.tensor.transpose(ps[:, k, m * P:(m + 1) * P], rows[:, m, k * P:(k + 1) * P], ident[:, :])
                    if m == MT // 2 - 1:
                        tr.then_inc(bank_full, 1)

            def x_second_half(k):
                if k == 0:
                    pe.wait_ge(x_scaled, MT)
                pe.wait_ge(dve_read, DR_X + k + 4 + 1)
                for c in range(4):
                    tr = nc.tensor.transpose(ps[:, 4 + k % 4, c * P:(c + 1) * P],
                                             rows[:, 4 + c, k * P:(k + 1) * P], ident[:, :])
                tr.then_inc(bank_full, 1)

            def v_tile(n, k, free=None, tiles=range(MT), first=0):
                pe.wait_ge(w_low_done, n * 8 + (k + 1))
                tokens_stationary(k, act_high[:, k], act_low[:, k], k == 0, k == KT - 1, free, tiles, first)

            def free_first(m):
                pe.wait_ge(dve_read, DR_X + m + 1)

            for k in range(RING):
                pe.wait_ge(dve_read, DR_X + k + 1)
                v_tile(0, k, free_first if k == 0 else None, range(4), first=4)
                if k >= RING - 2:
                    for kk in range(4 * (k - RING + 2), 4 * (k - RING + 3)):
                        x_second_half(kk)
            for k in range(RING):
                pe.wait_ge(dve_read, DR_X + KT + k + 1)

                def free_x(m):
                    pe.wait_ge(dve_read, DR_X + KT + m + 1)
                v_tile(0, k, free_x if k == 0 else None, range(4, MT), first=4)
            for k in range(RING, KT):
                v_tile(0, k)
            with pe.Fori(1, W // NB) as n:
                for k in range(KT):
                    def free_v(m):
                        pe.wait_ge(act_read, n * 8 + (AR_V - 7 + m))
                    v_tile(n, k, free_v if k == 0 else None)

            pe.wait_ge(ws_masked, 1)
            for i in range(2):
                pe.wait_ge(act_read, AR_U - 1 + i)
                for c in range(4):
                    tr = nc.tensor.transpose(ps[:, 6 + i, c * P:(c + 1) * P], ws_nat[:, 4 * i + c, :], ident[:, :])
                tr.then_inc(bank_full, 1)

            with pe.Fori(0, W // NB) as b:
                for k in range(KT):
                    pe.wait_ge(w_low_done, b * 8 + (8 * G_U + k + 1))

                    def free(i):
                        pe.wait_ge(act_read, b * 8 + (AR_U - 7 + i))
                        pe.wait_ge(dve_read, b * 8 + (DR_U - 7 + i))
                    weights_stationary(k, act_high[:, k], act_low[:, k], k == 0, k == KT - 1, free if k == 0 else None)
                pe.wait_ge(vn_done, b * 8 + 8)
                for i in range(BANKS):
                    pe.wait_ge(act_read, b * 8 + (AR_U + i + 1))
                    for c in range(4):
                        mm = nc.tensor.matmul(ps[:, i, c * P:(c + 1) * P], vn[:, 4 * (i % 2) + c, i // 2, :],
                                              ws_t[:, ds(b * 2 + i // 4, 1), :], start=True, stop=True)
                    mm.then_inc(bank_full, 1)

            for n in range(2):
                for e in range(JT):
                    t = JT * n + e
                    pe.wait_ge(w_low_done, 8 * G_OUT + t + 1)
                    pe.wait_ge(g_low_done, t + 1)

                    def free(m):
                        pe.wait_ge(dve_read, DR_OUT + 16 * n - 7 + m)
                    tokens_stationary(e, act_high[:, t % RING], act_low[:, t % RING], e == 0, e == JT - 1,
                                      free if e == 0 else None)
                for i in range(BANKS):
                    pe.wait_ge(dve_read, DR_OUT + 16 * n + (4 if i < 4 else 8))
                    for c in range(4):
                        kk = JB * n + i % JB
                        tr = nc.tensor.transpose(ps[:, i, c * P:(c + 1) * P],
                                                 rows[:, 4 * (i // JB) + c, kk * P:(kk + 1) * P], ident[:, :])
                    tr.then_inc(bank_full, 1)

            def hidden_products(b, s):
                for k in range(KT):
                    pe.wait_ge(w_low_done, b * 32 + s * 8 + (8 * G_MLP + k + 1))

                    def free(i):
                        pe.wait_ge(act_read, b * 16 + s * 8 + (AR_MLP - 7 + i))
                        pe.wait_ge(dve_read, b * 16 + (DR_MLP - 7 + i))
                    pe.wait_ge(dve_read, DR_OUT + 16 * (k // JB) + 8 + JB + k % JB + 1)
                    weights_stationary(k, act_high[:, phys(k)], act_low[:, phys(k)], k == 0, k == KT - 1,
                                       free if k == 0 else None)

            def output_free(b, n, m):
                pe.wait_ge(act_read, b * 16 + (AR_MLP + 8 + m + 1))
                pe.wait_ge(dve_read, b * 16 + n * 8 + (DR_MLP - 7 + m))

            def output_products(b, n):
                for f in range(KT):
                    pe.wait_ge(w_low_done, b * 32 + n * 8 + (8 * G_MLP + 16 + f + 1))
                    pe.wait_ge(hid_low_done, b * 16 + (SCRATCH + 2 * f + 2))
                    tokens_stationary(f, hid_high[:, f], hid_low[:, f], f == 0, f == KT - 1,
                                      (lambda m: output_free(b, n, m)) if f == 0 else None)

            with pe.Fori(0, MLP_BLOCKS - 1) as b:
                with pe.Fori(0, 2) as s:
                    hidden_products(b, s)
                with pe.Fori(0, 2) as n:
                    output_products(b, n)
            with pe.Fori(0, 2) as s:
                hidden_products(MLP_BLOCKS - 1, s)
            output_products(MLP_BLOCKS - 1, 0)
            pe.wait_ge(w_low_done, TILES)
            for m in range(MT):
                output_free(MLP_BLOCKS - 1, 1, m)
                c = slice(m * P, (m + 1) * P)
                for f in range(KT):
                    high, low = last_w(f)
                    products(m, hid_high[:, f, c], hid_low[:, f, c], high, low, f == 0, f == KT - 1,
                             m == 0 and f == 0)


_INS = ["x", "norm1_g", "norm2_g", "mlp_w1", "mlp_w2", "final_g", "a_w_in", "a_ln_g", "a_ws", "a_bs", "a_w_out"]


def kernel(**inputs):
    import numpy as _np
    import concourse.bacc as _bacc
    from concourse import mybir as _mybir
    from concourse.bass_utils import run_bass_kernel_spmd as _run

    nc = _bacc.Bacc("TRN2", target_bir_lowering=False, num_devices=1, dynamic_dma_scratch_size=4096)
    arrays, args = {}, []
    for name in _INS:
        a = _np.ascontiguousarray(inputs[name])
        arrays[f"in_{name}_dram"] = a
        args.append(nc.dram_tensor(f"in_{name}_dram", a.shape, _mybir.dt.from_np(a.dtype), kind="ExternalInput").ap())
    args.append(nc.dram_tensor("out_0_dram", (1, T, D), F32, kind="ExternalOutput").ap())
    trunk(nc, *args)
    r = _run(nc, [arrays], core_ids=[0])
    return r.results[0]["out_0_dram"]
```
